# Optimizing a Trainium2 kernel written in Bass

```python
import math
import jax, jax.numpy as jnp
from jax import lax
import numpy as np

D_MODEL = 2048
BATCH = 1
SEQ = 256
DEPTH = 1
DEC_BATCH = 8
DEC_SEQ = 8
PAST_LEN = 256
PAGE_SIZE = 128

GLA_HEADS = 4
GLA_DK = 128
GLA_DV = 256
GLA_KW = GLA_HEADS * GLA_DK
GLA_VW = GLA_HEADS * GLA_DV
GLA_RANK = 16
GLA_TAU = 16.0
GLA_CHUNK = 64
FOX_HEADS = 8
FOX_DH = 128
FOX_W = FOX_HEADS * FOX_DH
FOX_BLOCK = 128
D_FF = ((8 * D_MODEL + 3 * 256 - 1) // (3 * 256)) * 256
EPS = 1e-6
IN_SPLITS = (GLA_KW, GLA_KW, GLA_VW, GLA_VW, GLA_RANK, FOX_W, FOX_W, FOX_W, FOX_HEADS, D_MODEL, D_MODEL)
D_IN = 2 * GLA_KW + 2 * GLA_VW + GLA_RANK + 3 * FOX_W + FOX_HEADS + 2 * D_MODEL

kernel_name = 'gla_fox_parallel_hybrid_step'

def rmsnorm(x, g):
    xf = x.astype(jnp.float32)
    y = xf * lax.rsqrt(jnp.mean(xf * xf, axis=-1, keepdims=True) + EPS)
    return (y * g.astype(jnp.float32)).astype(x.dtype)

def branch_inputs(x, g_attn, w_in, w_gla_a2, b_gla_a, b_fox_f):
    B, L = x.shape[0], x.shape[1]
    f32 = jnp.float32
    z = rmsnorm(x, g_attn) @ w_in
    offs = [int(o) for o in np.cumsum(IN_SPLITS)[:-1]]
    gq, gk, gv, gr, ga1, fq, fk, fv, ff, gate_a, gate_b = jnp.split(z, offs, axis=-1)
    heads = lambda t, h, d: t.astype(f32).reshape(B, L, h, d)
    log_a = jax.nn.log_sigmoid((ga1 @ w_gla_a2 + b_gla_a).astype(f32)) / GLA_TAU
    lf = jax.nn.log_sigmoid((ff + b_fox_f).astype(f32))
    return (heads(gq, GLA_HEADS, GLA_DK) * GLA_DK ** -0.5, heads(gk, GLA_HEADS, GLA_DK),
            heads(gv, GLA_HEADS, GLA_DV), gr, heads(log_a, GLA_HEADS, GLA_DK),
            heads(fq, FOX_HEADS, FOX_DH), heads(fk, FOX_HEADS, FOX_DH), heads(fv, FOX_HEADS, FOX_DH),
            lf, gate_a, gate_b)

def gla_chunked(q, k, v, log_a, s0):
    B, L = q.shape[0], q.shape[1]
    C = math.gcd(L, GLA_CHUNK)
    n = L // C
    to_chunks = lambda t: t.reshape(B, n, C, t.shape[2], t.shape[3]).transpose(1, 0, 3, 2, 4)
    causal = jnp.tril(jnp.ones((C, C), dtype=bool))

    def step(S, inp):
        qi, ki, vi, ai = inp
        b = jnp.cumsum(ai, axis=-2)
        q_dec = qi * jnp.exp(b)
        k_inv = ki * jnp.exp(-b)
        attn = jnp.where(causal, jnp.einsum('bhtd,bhsd->bhts', q_dec, k_inv), 0.0)
        o = jnp.einsum('bhtd,bhdv->bhtv', q_dec, S) + jnp.einsum('bhts,bhsv->bhtv', attn, vi)
        k_end = ki * jnp.exp(b[..., -1:, :] - b)
        S = S * jnp.exp(b[..., -1, :])[..., None] + jnp.einsum('bhsd,bhsv->bhdv', k_end, vi)
        return S, o

    S_fin, o = lax.scan(step, s0.astype(jnp.float32), (to_chunks(q), to_chunks(k), to_chunks(v), to_chunks(log_a)))
    o = o.transpose(1, 0, 3, 2, 4).reshape(B, L, q.shape[2], v.shape[3])
    return o, S_fin

def fox_prompt(q, k, v, lf):
    B, S, H, Dh = q.shape
    nb = S // FOX_BLOCK
    c = jnp.cumsum(lf, axis=1)
    cT = c.transpose(0, 2, 1)
    pos = jnp.arange(S)
    qb = q.reshape(B, nb, FOX_BLOCK, H, Dh).transpose(1, 0, 2, 3, 4)
    cb = cT.reshape(B, H, nb, FOX_BLOCK).transpose(2, 0, 1, 3)
    pb = pos.reshape(nb, FOX_BLOCK)
    scale = FOX_DH ** -0.5

    def block(args):
        qi, ci, pi = args
        s = jnp.einsum('bqhd,bkhd->bhqk', qi, k) * scale + (ci[..., None] - cT[:, :, None, :])
        s = jnp.where(pi[:, None] >= pos[None, :], s, -jnp.inf)
        p = jax.nn.softmax(s, axis=-1)
        return jnp.einsum('bhqk,bkhd->bqhd', p, v)

    o = lax.map(block, (qb, cb, pb))
    return o.transpose(1, 0, 2, 3, 4).reshape(B, S, H, Dh)

def fox_sample(q, k, v, lf, k_cache, v_cache, lf_cache, page_table):
    B, T, H, Dh = q.shape
    n_pages = page_table.shape[1]
    scale = FOX_DH ** -0.5
    lf_past = lf_cache[page_table].astype(jnp.float32).reshape(B, n_pages * PAGE_SIZE, H)
    c_past = jnp.cumsum(lf_past, axis=1)
    c_past = c_past - c_past[:, -1:, :]
    cq = jnp.cumsum(lf, axis=1).transpose(0, 2, 1)
    c_pages = c_past.reshape(B, n_pages, PAGE_SIZE, H).transpose(1, 0, 3, 2)

    def page_step(carry, inp):
        m, l, acc = carry
        pt, cp = inp
        kp = k_cache[pt].astype(jnp.float32)
        vp = v_cache[pt].astype(jnp.float32)
        s = jnp.einsum('bthd,bphd->bhtp', q, kp) * scale + (cq[..., None] - cp[:, :, None, :])
        m_new = jnp.maximum(m, s.max(axis=-1))
        corr = jnp.exp(m - m_new)
        p = jnp.exp(s - m_new[..., None])
        return (m_new, l * corr + p.sum(axis=-1), acc * corr[..., None] + jnp.einsum('bhtp,bphd->bhtd', p, vp)), None

    init = (jnp.full((B, H, T), -jnp.inf, jnp.float32), jnp.zeros((B, H, T), jnp.float32),
            jnp.zeros((B, H, T, Dh), jnp.float32))
    (m, l, acc), _ = lax.scan(page_step, init, (page_table.T, c_pages))
    s = jnp.einsum('bthd,bshd->bhts', q, k) * scale + (cq[..., None] - cq[:, :, None, :])
    s = jnp.where(jnp.tril(jnp.ones((T, T), dtype=bool)), s, -jnp.inf)
    m_new = jnp.maximum(m, s.max(axis=-1))
    corr = jnp.exp(m - m_new)
    p = jnp.exp(s - m_new[..., None])
    l = l * corr + p.sum(axis=-1)
    acc = acc * corr[..., None] + jnp.einsum('bhts,bshd->bhtd', p, v)
    return (acc / l[..., None]).transpose(0, 2, 1, 3)

def layer_tail(x, o_gla, gr, o_fox, gate_a, gate_b, g_gla_norm, w_pa, w_pb, w_o, g_ffn, w_gate, w_up, w_down):
    B, L = x.shape[0], x.shape[1]
    o_gla = o_gla * lax.rsqrt(jnp.mean(o_gla * o_gla, axis=-1, keepdims=True) + EPS)
    o_gla = (o_gla.reshape(B, L, GLA_VW) * g_gla_norm.astype(jnp.float32)).astype(x.dtype) * jax.nn.silu(gr)
    o_fox = o_fox.reshape(B, L, FOX_W).astype(x.dtype)
    merged = jax.nn.sigmoid(gate_a) * (o_gla @ w_pa) + jax.nn.sigmoid(gate_b) * (o_fox @ w_pb)
    x = x + merged @ w_o
    h = rmsnorm(x, g_ffn)
    return x + (jax.nn.silu(h @ w_gate) * (h @ w_up)) @ w_down

def setup_inputs(seed: int = 0) -> dict:
    key = jax.random.key(seed)
    ks = jax.random.split(key, 24)
    f32 = jnp.float32
    n_pages = PAST_LEN // PAGE_SIZE
    n_pool = (DEC_BATCH * n_pages * 5) // 4
    nrm = lambda k, shape, scale: jax.random.normal(k, shape, f32) * scale
    gain = lambda k, shape: 1.0 + 0.02 * jax.random.normal(k, shape, f32)
    page_table = jax.random.permutation(ks[6], n_pool)[: DEC_BATCH * n_pages].reshape(DEC_BATCH, n_pages).astype(jnp.int32)
    return {
        'x_prompt': nrm(ks[0], (BATCH, SEQ, D_MODEL), 1.0),
        'x_sample': nrm(ks[1], (DEC_BATCH, DEC_SEQ, D_MODEL), 1.0),
        'cache_k': nrm(ks[2], (DEPTH, n_pool, PAGE_SIZE, FOX_HEADS, FOX_DH), 1.0),
        'cache_v': nrm(ks[3], (DEPTH, n_pool, PAGE_SIZE, FOX_HEADS, FOX_DH), 1.0),
        'cache_lf': jax.nn.log_sigmoid(2.0 + jax.random.normal(ks[4], (DEPTH, n_pool, PAGE_SIZE, FOX_HEADS), f32)),
        'state_gla': nrm(ks[5], (DEPTH, DEC_BATCH, GLA_HEADS, GLA_DK, GLA_DV), 0.5),
        'page_table': page_table,
        'g_attn': gain(ks[7], (DEPTH, D_MODEL)),
        'w_in': nrm(ks[8], (DEPTH, D_MODEL, D_IN), D_MODEL ** -0.5),
        'w_gla_a2': nrm(ks[9], (DEPTH, GLA_RANK, GLA_KW), GLA_RANK ** -0.5),
        'b_gla_a': nrm(ks[10], (DEPTH, GLA_KW), 0.1),
        'b_fox_f': 2.0 + nrm(ks[11], (DEPTH, FOX_HEADS), 0.1),
        'g_gla_norm': gain(ks[12], (DEPTH, GLA_VW)),
        'w_pa': nrm(ks[13], (DEPTH, GLA_VW, D_MODEL), GLA_VW ** -0.5),
        'w_pb': nrm(ks[14], (DEPTH, FOX_W, D_MODEL), FOX_W ** -0.5),
        'w_o': nrm(ks[15], (DEPTH, D_MODEL, D_MODEL), D_MODEL ** -0.5),
        'g_ffn': gain(ks[16], (DEPTH, D_MODEL)),
        'w_gate': nrm(ks[17], (DEPTH, D_MODEL, D_FF), D_MODEL ** -0.5),
        'w_up': nrm(ks[18], (DEPTH, D_MODEL, D_FF), D_MODEL ** -0.5),
        'w_down': nrm(ks[19], (DEPTH, D_FF, D_MODEL), D_FF ** -0.5),
        'g_final': gain(ks[20], (D_MODEL,)),
    }

def reference(x_prompt, x_sample, cache_k, cache_v, cache_lf, state_gla, page_table, g_attn, w_in, w_gla_a2,
              b_gla_a, b_fox_f, g_gla_norm, w_pa, w_pb, w_o, g_ffn, w_gate, w_up, w_down, g_final):
    yp, ys = x_prompt, x_sample
    s_p, s_s, k_p, v_p, lf_p, k_s, v_s, lf_s = ([] for _ in range(8))
    for l in range(DEPTH):
        tail_w = (g_gla_norm[l], w_pa[l], w_pb[l], w_o[l], g_ffn[l], w_gate[l], w_up[l], w_down[l])
        gq, gk, gv, gr, log_a, fq, fk, fv, lf, ga, gb = branch_inputs(yp, g_attn[l], w_in[l], w_gla_a2[l], b_gla_a[l], b_fox_f[l])
        s0 = jnp.zeros((yp.shape[0], GLA_HEADS, GLA_DK, GLA_DV), jnp.float32)
        o_a, s_fin = gla_chunked(gq, gk, gv, log_a, s0)
        o_b = fox_prompt(fq, fk, fv, lf)
        yp = layer_tail(yp, o_a, gr, o_b, ga, gb, *tail_w)
        s_p.append(s_fin)
        k_p.append(fk)
        v_p.append(fv)
        lf_p.append(lf)
        gq, gk, gv, gr, log_a, fq, fk, fv, lf, ga, gb = branch_inputs(ys, g_attn[l], w_in[l], w_gla_a2[l], b_gla_a[l], b_fox_f[l])
        o_a, s_fin = gla_chunked(gq, gk, gv, log_a, state_gla[l])
        o_b = fox_sample(fq, fk, fv, lf, cache_k[l], cache_v[l], cache_lf[l], page_table)
        ys = layer_tail(ys, o_a, gr, o_b, ga, gb, *tail_w)
        s_s.append(s_fin)
        k_s.append(fk)
        v_s.append(fv)
        lf_s.append(lf)
    y_prompt = rmsnorm(yp, g_final)
    y_sample = rmsnorm(ys, g_final)
    return (y_prompt, y_sample, jnp.stack(s_p), jnp.stack(s_s), jnp.stack(k_p), jnp.stack(v_p), jnp.stack(lf_p),
            jnp.stack(k_s), jnp.stack(v_s), jnp.stack(lf_s))


_drawn_inputs = setup_inputs


def setup_inputs(seed=0):
    import zlib

    import numpy as np

    out = dict(_drawn_inputs(seed))
    spreads = {}
    factors = {'g_gla_norm': 8.0, 'g_ffn': 4.158, 'g_final': 8.266, 'cache_lf': 3.441}
    for name, (base, spread) in spreads.items():
        noise = np.random.default_rng([zlib.crc32(name.encode()), seed]).standard_normal(out[name].shape)
        drawn = base * np.exp(spread * noise) if base else spread * noise
        out[name] = __import__('jax').numpy.asarray(drawn.astype(out[name].dtype))
    for name, factor in factors.items():
        out[name] = (out[name] * factor).astype(out[name].dtype)
    return out
```

```python
from contextlib import ExitStack

import concourse.bass as bass
from concourse import mybir

F32 = mybir.dt.float32
F32R = mybir.dt.float32r
I32 = mybir.dt.int32
I8 = mybir.dt.int8
ALU = mybir.AluOpType
ACT = mybir.ActivationFunctionType
AX = mybir.AxisListType.X
ds = bass.ds

P = 128
EPS = 1e-6
NEVER = -3.0e38
SLOTS = 4
LEAD = 2
UNIT = 8

HEAD = 2
START = 1

SCALAR_STEPS = 1
VECTOR_STEPS = {"project": 25, "merge": 4, "out": 4, "chunk": 38, "gate": 2, "down": 2, "down_final": 4}


SIGNALS = """
weights_landed_0 weights_landed_1 weights_landed_2 weights_landed_3
pages_landed x_landed_2 narrow_cleared low_ready lf_past_landed start_done fox_pv_done states_landed
gla_inter_done state_prompt_stored fox_qk_done keys_landed state_sample_stored values_landed y_stored y_scaled_2
pool_steps ident_ready constants_ready lf_tok_ready lf_stored gla_states_ready gla_states_s_ready
fox_tokens_ready kv_stored units_multiplied jobs_read slabs_used scalar_steps high_ready gains_landed a2_landed
stat_cleared x_squared x_mean_ready x_rstd_rough gains_ready x_turned x_high_ready z_row_ready e_row_ready
z_all_ready e_all_ready fox_out_read decay_ready to_end_ready swish_exp_ready gla_turned gla_v_ready gla_squares
gla_mean_ready gla_rstd_rough gla_out_ready gla_high_ready fox_keys_turned fox_keys_ready fox_tok_copies
fox_max_ready fox_exp_ready fox_probs_turned fox_probs_t_ready fox_max_s_ready fox_exp_s_ready
fox_probs_s_turned fox_probs_st_ready fox_high_ready merged_ready sig_ready merged_high_ready resid_ready
square_ready scaled_ready scaled_high_ready ffn_mean_ready ffn_rstd_rough gate_ready silu_ready hidden_ready
hidden_high_ready resid_final y_turned y_copied y_mean_ready y_rstd_rough y_rstd_ready y_scaled_1 vector_steps
gla_attn_ready gla_intra_done gla_sum_ready gla_sum_spread gla_low_ready fox_rows_ready fox_logits_done
fox_probs_ready fox_scores_t_ready fox_rows_done fox_probs_s_ready x_scaled gains_turned x_low_ready ga1_ready
c_rows_ready a2_multiplied c_turned merged_low_ready scaled_low_ready sum_ready sum_spread hidden_low_ready
y_feat_ready sum_by_token y_scaled_0 x_landed_0 x_landed_1 narrow_landed_0 narrow_landed_1 slab_landed_0
slab_landed_1
""".split()


class Unit:

    def __init__(self, first, quads=0):
        self.first, self.quads = first, quads
        self.slot = first % SLOTS

    def plus(self, n):
        return Unit(self.first + n, self.quads)

    def upto(self, n=0):
        return self.quads * SLOTS + (self.first + 1 + n)

    def landed(self):
        return self.quads * 16 + 16 * ((self.first - 2) // SLOTS + 1)


class Steps:

    def __init__(self, engine, semaphore):
        self.engine, self.semaphore, self.base, self.n, self.stack = engine, semaphore, 0, 0, []

    def then_wait(self, instruction):
        instruction.then_inc(self.semaphore, 1)
        self.n += 1
        self.engine.wait_ge(self.semaphore, self.base + self.n)

    def enter(self, turn, per):
        self.stack.append((self.base, self.n, per))
        self.base, self.n = self.base + self.n + turn * per, 0

    def leave(self, turns, name):
        base, n, per = self.stack.pop()
        assert self.n == per, f"{name}: {self.n} own steps in a turn, not {per}"
        self.base, self.n = base, n + turns * per


def hybrid_step(nc, x_prompt, x_sample, cache_k, cache_v, cache_lf, state_gla, page_table, g_attn, w_in, w_gla_a2,
                b_gla_a, b_fox_f, g_gla_norm, w_pa, w_pb, w_o, g_ffn, w_gate, w_up, w_down, g_final,
                y_prompt, y_sample, state_prompt, state_sample, k_prompt, v_prompt, lf_prompt,
                k_sample, v_sample, lf_sample):
    D = x_prompt.shape[2]
    SEQ = x_prompt.shape[1]
    NB, NT = x_sample.shape[0], x_sample.shape[1]
    SAMPLE = NB * NT
    T = SEQ + SAMPLE
    GH, DK, DV = state_gla.shape[2], state_gla.shape[3], state_gla.shape[4]
    FH, DH = cache_k.shape[3], cache_k.shape[4]
    POOL, PAGE = cache_k.shape[1], cache_k.shape[2]
    PAGES = page_table.shape[1]
    RANK = w_gla_a2.shape[1]
    F = w_gate.shape[2]
    KT = D // P
    VT = DV // P
    CH = 64
    NC = SEQ // CH
    FT = F // P
    CHUNKS = 4
    CT = FT // CHUNKS
    assert (D, SEQ, SAMPLE, GH, DK, DV, FH, DH, PAGE, PAGES) == (2048, 256, 64, 4, 128, 256, 8, 128, 128, 2)
    assert FT % CHUNKS == 0 and CT == 11 and cache_k.shape[0] == 1 and x_prompt.shape[0] == 1

    GQ = 0
    GK = GQ + GH * DK
    GV = GK + GH * DK
    GR = GV + GH * DV
    GA1 = GR + GH * DV
    FQ = GA1 + RANK
    FK = FQ + FH * DH
    FV = FK + FH * DH
    FF = FV + FH * DH
    GATE_A = FF + FH
    GATE_B = GATE_A + D
    assert GATE_B + D == w_in.shape[2]

    TURNS, JOBS = GH, 20
    U_PROJECT = 2
    U_MERGE = U_PROJECT + TURNS * JOBS * 2
    U_OUT = U_MERGE + 2 * KT
    U_FFN = U_OUT + 2 * KT
    U_CHUNK = 4 * CT + 2 * KT
    J_PROJECT = 1
    J_MERGE = J_PROJECT + TURNS * JOBS
    J_OUT = J_MERGE + 2 * KT
    J_FFN = J_OUT + KT
    J_CHUNK = 2 * CT + KT

    w_in_v = w_in[0].rearrange("(k p) n -> p k n", p=P)
    w_pa_v = w_pa[0].rearrange("(k p) n -> p k n", p=P)
    w_pb_v = w_pb[0].rearrange("(k p) n -> p k n", p=P)
    w_o_v = w_o[0].rearrange("(k p) n -> p k n", p=P)
    w_gate_v = w_gate[0].rearrange("(k p) n -> p k n", p=P)
    w_up_v = w_up[0].rearrange("(k p) n -> p k n", p=P)
    w_down_v = w_down[0].rearrange("(c k p) n -> c p k n", p=P, k=CT)
    x_sample_v = x_sample.rearrange("b t d -> (b t) d")
    x_prompt_v = x_prompt[0].rearrange("(k p) d -> p k d", p=P)
    y_sample_v = y_sample.rearrange("b t d -> (b t) d")
    y_prompt_v = y_prompt[0].rearrange("(k p) d -> p k d", p=P)
    k_prompt_v = k_prompt[0, 0].rearrange("(k p) h d -> p k h d", p=P)
    v_prompt_v = v_prompt[0, 0].rearrange("(k p) h d -> p k h d", p=P)
    k_sample_v = k_sample[0].rearrange("b t h d -> (b t) h d")
    v_sample_v = v_sample[0].rearrange("b t h d -> (b t) h d")

    with ExitStack() as ctx:
        def sb(name, shape, dt=F32):
            return ctx.enter_context(nc.sbuf_tensor(name, shape, dt))

        raw = sb("weights_raw", [P, SLOTS, UNIT * P])
        high = sb("weights_high", [P, SLOTS, UNIT * P], F32R)
        low = sb("weights_low", [P, SLOTS, UNIT * P], F32R)
        a_high = sb("a_high", [P, KT, T], F32R)
        a_low = sb("a_low", [P, KT, T], F32R)
        b_high = sb("b_high", [P, KT, T], F32R)
        b_low = sb("b_low", [P, KT, T], F32R)
        gates = sb("gates", [P, 2 * KT, T])
        tail = gates[:, 2 * KT - 8:2 * KT, :].rearrange("p a b -> p (a b)")
        decay_all = tail[:, 0:GH * T].rearrange("p (h t) -> p h t", h=GH)
        gla_v = tail[0:CH, GH * T:GH * T + (NC + 1) * DV].rearrange("p (c v) -> p c v", c=NC + 1)
        x_tok = gates[:, 0:20, :].rearrange("p a b -> p (a b)")[:, 0:3 * D].rearrange("p (k d) -> p k d", k=3)
        resid = gates
        fox_qkv = sb("fox_qkv", [P, 2, 3, T])
        attn_gla = sb("attn_gla", [CH, NC + 1, CH])
        area = sb("area", [P, 6720])

        def part(at, *shape, rows=P, start=0):
            n = 1
            for s in shape:
                n *= s
            v = area[start:start + rows, at:at + n]
            if len(shape) == 2:
                v = v.rearrange("p (a b) -> p a b", a=shape[0])
            elif len(shape) == 3:
                v = v.rearrange("p (a b c) -> p a b c", a=shape[0], b=shape[1])
            return v

        k_end = part(0, NC, DK, rows=CH)
        k_end_late = part(512, NB // 2, DK, rows=CH)
        states = part(1024, NC, DV)
        states_s = part(2048, NB, DV)
        decay = part(4096, T)
        q_dec = part(4416, T)
        k_inv = part(4736, T)
        k_end_f = part(5056, T)
        v_f = part(5376, VT, T)
        k_end_early = part(5376, NB // 2, DK, rows=CH)
        squares = part(5376, VT, T)
        o_gla = part(5376, VT, T)
        silu_r = part(6016, VT, T)
        keys = part(0, NB * PAGES, DH)
        values = part(2048, NB * PAGES, DH)
        k_tok = part(4096, 3, DH)
        v_tok = part(4480, 3, DH)
        probs = part(4864, 3 * P)
        probs_t = part(5248, 3, P)
        probs_s = part(5632, SAMPLE * 5, rows=SAMPLE)
        probs_st = part(5952, 3, SAMPLE)
        scores_t = part(6144, PAGES, SAMPLE)
        lf_wide = part(6272, PAGES, SAMPLE)
        neg_c = part(6400, T, rows=FH)
        junk = part(0, D)
        g_rows = part(2048, P, rows=60)
        w_a2 = part(2176, GH * DK, rows=RANK, start=32)
        scan_gla = part(2688, T)
        scan_fox = part(3008, T, rows=FH)
        ga1 = part(3328, T, rows=RANK, start=32)
        lf_rows = part(3648, T, rows=FH)
        z_all = part(4000, GH, T)
        e_all = part(5280, GH, T)
        lf_tok = part(6560, 3, FH)
        z_row = part(0, T, rows=FH)
        e_row = part(320, T, rows=FH)
        sig = part(0, 2, T)
        prod_a = part(640, T)
        prod_b = part(960, T)
        merged = part(1280, T)
        x_slab = part(1600, 2, 3, P)
        square = part(2400, T)
        sum_sq = part(2720, T)
        scaled = part(3040, T)
        rstd = part(3360, T)
        rtmp = part(3680, T)
        mean = part(4000, T)
        gate_s = part(640, T)
        silu_g = part(960, T)
        up_s = part(1280, T)
        hidden = part(4320, T)
        y_feat = part(0, 2, T)
        y_tok = gates[:, KT:2 * KT, :].rearrange("p a b -> p (a b)")[:, 0:2 * D].rearrange("p (k d) -> p k d", k=2)
        y_tok_s = part(4640, D, rows=SAMPLE)

        ident = sb("ident", [P, P])
        ones = sb("ones", [P, P])
        later = sb("later", [P, P])
        causal = sb("causal", [P, P])
        causal_s = sb("causal_s", [SAMPLE, SAMPLE])
        keep_gla = sb("keep_gla", [CH, NC + 1, CH], I8)
        own_rows = sb("own_rows", [SAMPLE, NB])
        minus_head = sb("minus_head", [FH, FH])
        gains = sb("gains", [P, 60])
        bias_ff = part(6600, 1, rows=FH)
        pages = sb("pages", [1, NB * PAGES], I32)
        lf_past = sb("lf_past", [P, NB * PAGES, FH])
        c_rows = sb("c_rows", [FH, T])
        c_tok = sb("c_tok", [P, 3, FH])
        stat = sb("stat", [P, 16])
        G_ATTN, G_FFN, G_FINAL, G_GLA, B_GLA = 0, KT, 2 * KT, 3 * KT, 3 * KT + GH * VT

        psum = ctx.enter_context(nc.psum_tensor("banks", [P, 8, 512], F32))

        def bank(b, a=0, n=512, rows=P):
            return psum[0:rows, b, a:a + n]

        def bank3(b, a, m, n, rows=P):
            return psum[0:rows, b, a:a + m * n].rearrange("p (m n) -> p m n", m=m)

        on = {name: ctx.enter_context(nc.semaphore(name)) for name in SIGNALS}
        landed = [on[f"weights_landed_{s}"] for s in range(SLOTS)]

        block = ctx.enter_context(nc.Block())

        def project_jobs():
            jobs = [(GQ, DK), (GK, DK)]
            jobs += [(GV + j * P, DV) for j in range(VT)]
            jobs += [(GR + j * P, DV) for j in range(VT)]
            for j in range(2):
                jobs += [(c + j * DH, 2 * DH) for c in (FQ, FK, FV)]
            jobs += [(c + r * P, 4 * P) for c in (GATE_A, GATE_B) for r in range(4)]
            return jobs

        KEYS_AT = (17, 25)
        VALUES_AT = (23, 31)
        FOX_AT = (19, 27)

        @block.sync
        def _(sp):
            sp.dma_start(pages[:, :], page_table.rearrange("b g -> (b g)").rearrange("(o n) -> o n", o=1)
                         ).then_inc(on["pages_landed"], 16)
            for k in range(2):
                sp.dma_start(x_tok[:, k, :], x_prompt_v[:, k, :]).then_inc(on[f"x_landed_{k}"], 16)
            sp.dma_start(x_tok[0:SAMPLE, 2, :], x_sample_v).then_inc(on["x_landed_2"], 16)
            sp.wait_ge(on["narrow_cleared"], 1)
            for u in range(2):
                slot = raw[:, u, :].rearrange("p (k n) -> p k n", k=UNIT)
                rows = slice(u * UNIT, (u + 1) * UNIT)
                sp.dma_start(slot[:, :, 0:FH], w_in_v[:, rows, FF:FF + FH]).then_inc(on[f"narrow_landed_{u}"], 16)
                sp.dma_start(slot[:, :, 32:32 + RANK], w_in_v[:, rows, GA1:GA1 + RANK]).then_inc(on[f"narrow_landed_{u}"], 16)

            def load(unit, source, tiles=UNIT):
                if unit.first >= HEAD:
                    sp.wait_ge(on["low_ready"], unit.upto(HEAD - SLOTS))
                sp.dma_start(raw[:, unit.slot, 0:tiles * P].rearrange("p (k n) -> p k n", k=tiles), source
                             ).then_inc(landed[unit.slot], 16)

            def half(view, h, col):
                return view[:, h * UNIT:(h + 1) * UNIT, ds(col, P)]

            sp.wait_ge(on["pages_landed"], 16)

            def page(n):
                return ds(sp.value_load(pages[0:1, n:n + 1], min_val=0, max_val=POOL - 1), 1)

            for n in range(NB * PAGES):
                sp.dma_start(lf_past[:, n, :], cache_lf[0, page(n), :, :].rearrange("o k h -> (o k) h")
                             ).then_inc(on["lf_past_landed"], 16)

            with sp.Fori(0, TURNS) as i:
                first = {
                    KEYS_AT[0]: [("gla_inter_done", i + 1), ("state_prompt_stored", i * 16 + 16)],
                    VALUES_AT[0]: [("state_sample_stored", i * 16 + 16)],
                    KEYS_AT[1]: [("fox_qk_done", i * 2 + 1)],
                    VALUES_AT[1]: [("fox_pv_done", i * 2 + (1 + START))],
                }
                for s in range(2 * JOBS):
                    col, step = project_jobs()[s // 2]
                    load(Unit(U_PROJECT + s, i * (2 * JOBS // SLOTS)), half(w_in_v, s % 2, i * step + col))
                    if s == 4:
                        sp.wait_ge(on["start_done"], 1)
                        sp.wait_ge(on["fox_pv_done"], i * 2 + START)
                        sp.dma_start(states_s, state_gla[0, :, ds(i, 1), :, :].rearrange("b o k v -> k (b o) v")
                                     ).then_inc(on["states_landed"], 16)
                    for j in range(2):
                        for at, cache, out, name in ((KEYS_AT[j], cache_k, keys, "keys_landed"),
                                                     (VALUES_AT[j], cache_v, values, "values_landed")):
                            if at <= s < at + 4:
                                n0 = 4 * (s - at)
                                four = [page(n0 + n) for n in range(4)]
                                for signal, value in first.get(s, []):
                                    sp.wait_ge(on[signal], value)
                                for n in range(4):
                                    sp.dma_start(out[:, n0 + n, :], cache[0, four[n], :, ds(i * 2 + j, 1), :].rearrange(
                                        "o k h d -> (o k) (h d)")).then_inc(on[name], 16)

            with sp.Fori(0, KT // 4) as i:
                for r in range(4):
                    load(Unit(U_MERGE + 2 * r, i * 2), half(w_pa_v, 0, i * (4 * P) + r * P))
                    load(Unit(U_MERGE + 2 * r + 1, i * 2), half(w_pb_v, 0, i * (4 * P) + r * P))

            sp.wait_ge(on["fox_pv_done"], FH + START)
            with sp.Fori(0, KT // 2) as i:
                for s in range(4):
                    r = s // 2
                    if s % 2 == 0:
                        sp.wait_ge(on["slabs_used"], i * 2 + (r + START))
                        sp.dma_start(x_slab[:, r, 0:2, :], x_prompt_v[:, :, ds(i * (2 * P) + r * P, P)]
                                     ).then_inc(on[f"slab_landed_{r}"], 16)
                        sp.dma_start(x_slab[0:SAMPLE, r, 2, :], x_sample_v[:, ds(i * (2 * P) + r * P, P)]
                                     ).then_inc(on[f"slab_landed_{r}"], 16)
                    load(Unit(U_OUT + s, i), half(w_o_v, s % 2, i * (2 * P) + r * P))

            with sp.Fori(0, CHUNKS) as c:
                with sp.Fori(0, CT) as f:
                    for s in range(4):
                        load(Unit(U_FFN + s, c * (U_CHUNK // 4) + f),
                             half((w_gate_v, w_up_v)[s // 2], s % 2, c * (CT * P) + f * P))
                with sp.Fori(0, KT // 2) as m:
                    for s in range(4):
                        a, n = ((0, 6), (6, 5))[s % 2]
                        load(Unit(U_FFN + 4 * CT + s, c * (U_CHUNK // 4) + m),
                             w_down_v[ds(c, 1), :, a:a + n, ds(m * (2 * P) + (s // 2) * P, P)].rearrange(
                                 "o p k n -> (o p) k n"), tiles=n)

            for k in range(2):
                sp.wait_ge(on[f"y_scaled_{k}"], 1)
                sp.dma_start(y_prompt_v[:, k, :], y_tok[:, k, :]).then_inc(on["y_stored"], 16)
            sp.wait_ge(on["y_scaled_2"], 1)
            sp.dma_start(y_sample_v, y_tok_s).then_inc(on["y_stored"], 16)
            sp.wait_ge(on["y_stored"], 48)

        @block.gpsimd
        def _(pool):
            own = Steps(pool, on["pool_steps"])
            own.then_wait(pool.memset(ident[:, :], 0.0))
            pool.affine_select(out=ident[:, :], in_=ident[:, :], compare_op=ALU.not_equal, fill=1.0, base=0,
                               pattern=[[-1, P]], channel_multiplier=1).then_inc(on["ident_ready"], 1)
            own.then_wait(pool.memset(ones[:, :], 1.0))
            own.then_wait(pool.affine_select(out=later[:, :], in_=ones[:, :], compare_op=ALU.is_gt, fill=0.0, base=0,
                                             pattern=[[-1, P]], channel_multiplier=1))
            own.then_wait(pool.memset(causal[:, :], 0.0))
            own.then_wait(pool.affine_select(out=causal[:, :], in_=causal[:, :], compare_op=ALU.is_ge, fill=NEVER,
                                             base=0, pattern=[[-1, P]], channel_multiplier=1))
            own.then_wait(pool.memset(causal_s[:, :], 0.0))
            for base, pattern, mult in ((0, [[-NT, NB], [0, NT]], 1), (NT - 1, [[NT, NB], [0, NT]], -1),
                                        (0, [[-1, SAMPLE]], 1)):
                own.then_wait(pool.affine_select(out=causal_s[:, :], in_=causal_s[:, :], compare_op=ALU.is_ge,
                                                 fill=NEVER, base=base, pattern=pattern, channel_multiplier=mult))
            own.then_wait(pool.memset(keep_gla[:, :, :], 1.0))
            own.then_wait(pool.affine_select(out=keep_gla[:, :, :], in_=keep_gla[:, :, :], compare_op=ALU.is_ge,
                                             fill=0.0, base=0, pattern=[[0, NC + 1], [1, CH]], channel_multiplier=-1))
            for base, pattern, mult in ((0, [[-NT, NB], [0, NT]], 1), (NT - 1, [[NT, NB], [0, NT]], -1)):
                own.then_wait(pool.affine_select(out=keep_gla[:, NC, :], in_=keep_gla[:, NC, :], compare_op=ALU.is_ge,
                                                 fill=0.0, base=base, pattern=pattern, channel_multiplier=mult))
            own.then_wait(pool.memset(own_rows[:, :], 1.0))
            for base, pattern, mult in ((0, [[-NT, NB]], 1), (NT - 1, [[NT, NB]], -1)):
                own.then_wait(pool.affine_select(out=own_rows[:, :], in_=own_rows[:, :], compare_op=ALU.is_ge,
                                                 fill=0.0, base=base, pattern=pattern, channel_multiplier=mult))
            own.then_wait(pool.memset(minus_head[:, :], 0.0))
            own.then_wait(pool.affine_select(out=minus_head[:, :], in_=minus_head[:, :], compare_op=ALU.not_equal,
                                             fill=-1.0, base=0, pattern=[[-1, FH]], channel_multiplier=1))
            own.then_wait(pool.memset(scan_gla, 1.0))
            own.then_wait(pool.memset(scan_gla[:, 0:SEQ].rearrange("p (c t) -> p c t", t=CH)[:, :, 0:1], 0.0))
            own.then_wait(pool.memset(scan_gla[:, SEQ:T].rearrange("p (c t) -> p c t", t=NT)[:, :, 0:1], 0.0))
            own.then_wait(pool.memset(scan_fox, 1.0))
            own.then_wait(pool.memset(scan_fox[:, 0:1], 0.0))
            pool.memset(scan_fox[:, SEQ:T].rearrange("p (c t) -> p c t", t=NT)[:, :, 0:1], 0.0
                        ).then_inc(on["constants_ready"], 1)

            pool.wait_ge(on["lf_tok_ready"], 1)
            pool.dma_start(lf_prompt[0, 0].rearrange("(k p) h -> p k h", p=P), lf_tok[:, 0:2, :]).then_inc(on["lf_stored"], 16)
            pool.dma_start(lf_sample[0].rearrange("b t h -> (b t) h"), lf_tok[0:SAMPLE, 2, :]).then_inc(on["lf_stored"], 16)

            pool.wait_ge(on["lf_stored"], 32)
            pool.wait_ge(on["state_prompt_stored"], 16 * TURNS)
            pool.wait_ge(on["state_sample_stored"], 16 * TURNS)
            pool.wait_ge(on["kv_stored"], 64 * FH + START)

        @block.scalar
        def _(act):
            own = Steps(act, on["scalar_steps"])
            act.preload_act_table_set("natural_log_exp_and_others")
            for name in ("kv_stored", "y_copied"):
                act.sem_inc(on[name], START)

            def prepare(unit, tiles=UNIT):
                if unit.first < 2:
                    act.wait_ge(on[f"narrow_landed_{unit.first}"], 32)
                else:
                    act.wait_ge(landed[unit.slot], unit.landed())
                if unit.first >= SLOTS:
                    act.wait_ge(on["units_multiplied"], unit.upto(-SLOTS))
                act.activation(high[:, unit.slot, 0:tiles * P], raw[:, unit.slot, 0:tiles * P], ACT.Copy
                               ).then_inc(on["high_ready"], 1)

            act.dma_start(g_rows[0:KT, :], g_attn[0].rearrange("(k p) -> k p", p=P)).then_inc(on["gains_landed"], 16)
            act.dma_start(g_rows[KT:2 * KT, :], g_ffn[0].rearrange("(k p) -> k p", p=P)).then_inc(on["gains_landed"], 16)
            act.dma_start(g_rows[2 * KT:3 * KT, :], g_final.rearrange("(k p) -> k p", p=P)).then_inc(on["gains_landed"], 16)
            act.dma_start(g_rows[3 * KT:3 * KT + 8, :], g_gla_norm[0].rearrange("(k p) -> k p", p=P)).then_inc(on["gains_landed"], 16)
            act.dma_start(g_rows[B_GLA:B_GLA + GH, :], b_gla_a[0].rearrange("(k p) -> k p", p=P)).then_inc(on["gains_landed"], 16)
            act.dma_start(w_a2, w_gla_a2[0]).then_inc(on["a2_landed"], 16)
            act.dma_start(bias_ff[:, :], b_fox_f.rearrange("o h -> h o")).then_inc(on["a2_landed"], 16)

            act.wait_ge(on["stat_cleared"], 1)
            for k in range(3):
                rows = P if k < 2 else SAMPLE
                act.wait_ge(on[f"x_landed_{k}"], 16)
                if k:
                    act.wait_ge(on["x_squared"], k)
                act.activation(junk[0:rows, :], x_tok[0:rows, k, :], ACT.Square, accum_out=stat[0:rows, k:k + 1]
                               ).then_inc(on["x_squared"], 1)
            act.wait_ge(on["x_mean_ready"], 1)
            own.then_wait(act.activation(stat[:, 3:6], stat[:, 0:3], ACT.Ln))
            act.activation(stat[:, 3:6], stat[:, 3:6], ACT.Exp, scale=-0.5).then_inc(on["x_rstd_rough"], 1)
            prepare(Unit(0))
            prepare(Unit(1))
            act.wait_ge(on["gains_ready"], 1)
            for m in range(KT):
                act.wait_ge(on["x_turned"], m + 1)
                act.activation(a_high[:, m, :], bank(2 + m % 4, 0, T), ACT.Copy, scale=gains[:, G_ATTN + m:G_ATTN + m + 1]
                               ).then_inc(on["x_high_ready"], 1)
            prepare(Unit(2))
            prepare(Unit(3))
            act.wait_ge(on["z_row_ready"], 1)
            own.then_wait(act.activation(e_row, z_row, ACT.Abs))
            own.then_wait(act.activation(e_row, e_row, ACT.Exp, scale=-1.0))
            act.activation(e_row, e_row, ACT.Ln, bias=1.0).then_inc(on["e_row_ready"], 1)
            for h in range(GH):
                act.wait_ge(on["z_all_ready"], h + 1)
                own.then_wait(act.activation(e_all[:, h, :], z_all[:, h, :], ACT.Abs))
                own.then_wait(act.activation(e_all[:, h, :], e_all[:, h, :], ACT.Exp, scale=-1.0))
                act.activation(e_all[:, h, :], e_all[:, h, :], ACT.Ln, bias=1.0).then_inc(on["e_all_ready"], 1)
            act.wait_ge(on["start_done"], 1)

            with act.Fori(0, TURNS) as i:
                own.enter(i, SCALAR_STEPS)
                for s in range(2 * JOBS):
                    unit = Unit(U_PROJECT + s, i * (2 * JOBS // SLOTS))
                    prepare(unit.plus(LEAD))
                    if s == 0:
                        act.wait_ge(on["kv_stored"], i * 128 + START)
                        act.wait_ge(on["fox_out_read"], i * 2 + START)
                        act.activation(decay, decay_all[:, ds(i, 1), :].rearrange("p o t -> p (o t)"), ACT.Exp
                                       ).then_inc(on["decay_ready"], 1)
                        act.activation(k_inv, decay_all[:, ds(i, 1), :].rearrange("p o t -> p (o t)"), ACT.Exp, scale=-1.0
                                       ).then_inc(on["decay_ready"], 1)
                        act.wait_ge(on["to_end_ready"], i + 1)
                        act.activation(k_end_f, k_end_f, ACT.Exp).then_inc(on["decay_ready"], 1)
                    if s in (10, 12):
                        j = (s - 10) // 2
                        act.wait_ge(on["units_multiplied"], unit.upto(-1))
                        act.activation(silu_r[:, j, :], bank((J_PROJECT + s // 2 - 1) % 2, 0, T), ACT.Exp, scale=-1.0
                                       ).then_inc(on["swish_exp_ready"], 1)
                    if s == 10:
                        act.wait_ge(on["gla_turned"], i + 1)
                        act.activation(gla_v[:, 0:2, :], bank3(2, 0, 2, DV, CH), ACT.Copy).then_inc(on["gla_v_ready"], 1)
                        act.activation(gla_v[:, 2:4, :], bank3(3, 0, 2, DV, CH), ACT.Copy).then_inc(on["gla_v_ready"], 1)
                        act.activation(gla_v[:, 4, :], bank(4, 0, DV, CH), ACT.Copy).then_inc(on["gla_v_ready"], 1)
                        act.activation(k_end, bank3(5, 0, 4, DK, CH), ACT.Copy).then_inc(on["gla_v_ready"], 1)
                    if s == 13:
                        act.wait_ge(on["gla_states_ready"], i + 1)
                        act.dma_start(state_prompt[0, 0, ds(i, 1), :, :].rearrange("o k v -> (o k) v"), states[:, NC - 1, :]
                                      ).then_inc(on["state_prompt_stored"], 16)
                    if s == 16:
                        act.wait_ge(on["gla_states_s_ready"], i + 1)
                        act.dma_start(state_sample[0, :, ds(i, 1), :, :].rearrange("b o k v -> k (b o) v"), states_s
                                      ).then_inc(on["state_sample_stored"], 16)
                    if s == 15:
                        act.wait_ge(on["gla_inter_done"], i + 1)
                        for j in range(VT):
                            act.activation(squares[:, j, :], bank(7 - j, 0, T), ACT.Square).then_inc(on["gla_squares"], 1)
                    if s == 17:
                        act.wait_ge(on["gla_mean_ready"], i + 1)
                        own.then_wait(act.activation(decay, k_end_f, ACT.Ln))
                        act.activation(decay, decay, ACT.Exp, scale=-0.5).then_inc(on["gla_rstd_rough"], 1)
                    if s == 19:
                        act.wait_ge(on["gla_out_ready"], i + 1)
                        act.activation(b_high[:, ds(i * 2, 2), :], o_gla, ACT.Copy).then_inc(on["gla_high_ready"], 1)
                    for j, at in enumerate(FOX_AT):
                        n = i * 2 + (j + 1)
                        if s == at + 1:
                            act.wait_ge(on["fox_keys_turned"], n * 2 - 1)
                            for r in range(2):
                                act.activation(keys[:, 4 * r:4 * r + 4, :], bank3(6 + r, 0, 4, DH), ACT.Copy
                                               ).then_inc(on["fox_keys_ready"], 1)
                            act.wait_ge(on["kv_stored"], n * 64 - (64 - START))
                            for tok, b in ((k_tok, 2), (v_tok, 3)):
                                act.activation(tok[:, 0:2, :], bank3(b, 0, 2, DH), ACT.Copy).then_inc(on["fox_tok_copies"], 1)
                                act.activation(tok[0:SAMPLE, 2, :], bank(b, 2 * DH, DH, SAMPLE), ACT.Copy
                                               ).then_inc(on["fox_tok_copies"], 1)
                            act.wait_ge(on["fox_tok_copies"], n * 4)
                            act.sem_inc(on["fox_tokens_ready"], 1)
                        if s == at + 2:
                            for tok, whole, few in ((k_tok, k_prompt_v, k_sample_v), (v_tok, v_prompt_v, v_sample_v)):
                                act.dma_start(whole[:, :, ds(i * 2 + j, 1), :].rearrange("p k o d -> p k (o d)"), tok[:, 0:2, :]
                                              ).then_inc(on["kv_stored"], 16)
                                act.dma_start(few[:, ds(i * 2 + j, 1), :].rearrange("p o d -> p (o d)"), tok[0:SAMPLE, 2, :]
                                              ).then_inc(on["kv_stored"], 16)
                            act.wait_ge(on["fox_max_ready"], n)
                            act.activation(probs[:, 0:P], probs[:, 0:P], ACT.Exp, bias=stat[:, 6:7], accum_out=stat[:, 8:9]
                                           ).then_inc(on["fox_exp_ready"], 1)
                            act.activation(probs[:, P:3 * P], probs[:, P:3 * P], ACT.Exp, bias=stat[:, 7:8],
                                           accum_out=stat[:, 9:10]).then_inc(on["fox_exp_ready"], 1)
                            act.wait_ge(on["fox_keys_turned"], n * 2)
                            for r in range(2):
                                act.activation(keys[:, 8 + 4 * r:12 + 4 * r, :], bank3(6 + r, 0, 4, DH), ACT.Copy
                                               ).then_inc(on["fox_keys_ready"], 1)
                        if s == at + 4:
                            act.wait_ge(on["fox_probs_turned"], n)
                            act.activation(probs_t, bank3(4, 0, 3, P), ACT.Copy).then_inc(on["fox_probs_t_ready"], 1)
                            act.wait_ge(on["fox_max_s_ready"], n)
                            act.activation(probs_s, probs_s, ACT.Exp, bias=stat[0:SAMPLE, 10:11],
                                           accum_out=stat[0:SAMPLE, 11:12]).then_inc(on["fox_exp_s_ready"], 1)
                        if s == at + 6:
                            act.wait_ge(on["fox_probs_s_turned"], n)
                            act.activation(probs_st[:, 0:2, :], bank3(4, 0, 2, SAMPLE), ACT.Copy
                                           ).then_inc(on["fox_probs_st_ready"], 1)
                            act.activation(probs_st[0:SAMPLE, 2, :], bank(4, 2 * SAMPLE, SAMPLE, SAMPLE), ACT.Copy
                                           ).then_inc(on["fox_probs_st_ready"], 1)
                        if s == at + 7:
                            act.wait_ge(on["fox_pv_done"], n + START)
                            act.activation(b_high[:, ds(i * 2 + (8 + j), 1), :].rearrange("p o t -> p (o t)"), bank(3, 0, T),
                                           ACT.Copy).then_inc(on["fox_high_ready"], 1)
                own.leave(TURNS, "scalar, projection")

            with act.Fori(0, KT // 4) as i:
                for r in range(4):
                    for s in (2 * r, 2 * r + 1):
                        prepare(Unit(U_MERGE + s, i * 2).plus(LEAD))
                        if s == 2 * r:
                            act.wait_ge(on["merged_ready"], i * 4 + (r + START))
                            if r == 0:
                                act.wait_ge(on["jobs_read"], J_MERGE + START)
                            act.activation(sig, gates[:, ds(i * 8 + r, 5), :][:, 0:5:4, :], ACT.Sigmoid
                                           ).then_inc(on["sig_ready"], 1)
                    act.wait_ge(on["merged_ready"], i * 4 + (r + 1 + START))
                    act.activation(a_high[:, ds(i * 4 + r, 1), :].rearrange("p o t -> p (o t)"), merged, ACT.Copy
                                   ).then_inc(on["merged_high_ready"], 1)

            with act.Fori(0, KT // 2) as i:
                for r in range(2):
                    for s in (2 * r, 2 * r + 1):
                        prepare(Unit(U_OUT + s, i).plus(LEAD))
                    act.wait_ge(on["resid_ready"], i * 2 + (r + 1))
                    act.activation(square, resid[:, ds(i * 2 + r, 1), :].rearrange("p o t -> p (o t)"), ACT.Square
                                   ).then_inc(on["square_ready"], 1)
                    act.wait_ge(on["scaled_ready"], i * 2 + (r + 1))
                    act.activation(b_high[:, ds(i * 2 + r, 1), :].rearrange("p o t -> p (o t)"), scaled, ACT.Copy
                                   ).then_inc(on["scaled_high_ready"], 1)

            act.wait_ge(on["ffn_mean_ready"], 1)
            own.then_wait(act.activation(rstd, mean, ACT.Ln))
            act.activation(rstd, rstd, ACT.Exp, scale=-0.5).then_inc(on["ffn_rstd_rough"], 1)

            def chunk(c, final):
                unit0 = Unit(U_FFN, c * (U_CHUNK // 4))

                def gate_up(f, last):
                    unit = Unit(U_FFN, c * (U_CHUNK // 4) + f)
                    for s in range(4):
                        ahead = unit.plus(s + LEAD)
                        prepare(ahead, (6, 5)[s % 2] if last and s >= 2 else UNIT)
                        if s == 2:
                            act.wait_ge(on["gate_ready"], c * CT + f + 1)
                            act.activation(silu_g, gate_s, ACT.Silu).then_inc(on["silu_ready"], 1)
                    act.wait_ge(on["hidden_ready"], c * CT + f + 1)
                    act.activation(a_high[:, ds(f, 1), :].rearrange("p o t -> p (o t)"), hidden, ACT.Copy
                                   ).then_inc(on["hidden_high_ready"], 1)

                with act.Fori(0, CT - 1) as f:
                    gate_up(f, False)
                gate_up(CT - 1, True)

                def down(m, last, first=False):
                    unit = Unit(U_FFN + 4 * CT, c * (U_CHUNK // 4) + m)
                    for r in range(2):
                        for s in (2 * r, 2 * r + 1):
                            if not last or s < 2:
                                prepare(unit.plus(s + LEAD), (6, 5)[s % 2])
                            elif not final:
                                prepare(unit.plus(s + LEAD), UNIT)
                        if final:
                            act.wait_ge(on["resid_final"], m * 2 + (r + 1))
                            act.activation(square, resid[:, ds(m * 2 + r, 1), :].rearrange("p o t -> p (o t)"), ACT.Square
                                           ).then_inc(on["square_ready"], 1)
                            if r == 1 or not first:
                                y_copy(m * 2 + r, 1 - r)

                def y_copy(n, r):
                    act.wait_ge(on["y_turned"], n + START)
                    cols = ds(n * P - P, P)
                    act.activation(y_tok[:, :, cols], bank3(2 + r, 0, 2, P), ACT.Copy).then_inc(on["y_copied"], 1)
                    act.activation(y_tok_s[:, cols], bank(2 + r, 2 * P, P, SAMPLE), ACT.Copy).then_inc(on["y_copied"], 1)

                down(0, False, True)
                with act.Fori(1, KT // 2 - 1) as m:
                    down(m, False)
                down(KT // 2 - 1, True)
                if final:
                    y_copy(KT, 1)

            with act.Fori(0, CHUNKS - 1) as c:
                chunk(c, False)
            chunk(CHUNKS - 1, True)

            act.wait_ge(on["y_mean_ready"], 1)
            own.then_wait(act.activation(stat[:, 3:6], stat[:, 0:3], ACT.Ln))
            act.activation(stat[:, 3:6], stat[:, 3:6], ACT.Exp, scale=-0.5).then_inc(on["y_rstd_rough"], 1)
            act.wait_ge(on["y_rstd_ready"], 1)
            act.wait_ge(on["y_copied"], 2 * KT + START)
            act.activation(y_tok[:, 1, :], y_tok[:, 1, :], ACT.Copy, scale=stat[:, 4:5]).then_inc(on["y_scaled_1"], 1)

        @block.vector
        def _(dve):
            own = Steps(dve, on["vector_steps"])
            link = own.then_wait

            def prepare(unit, tiles=UNIT):
                dve.wait_ge(on["high_ready"], unit.upto())
                n = tiles * P
                dve.tensor_tensor(low[:, unit.slot, 0:n], raw[:, unit.slot, 0:n], high[:, unit.slot, 0:n].bitcast(F32),
                                  ALU.subtract).then_inc(on["low_ready"], 1)

            def refine(y, x, t):
                link(dve.tensor_tensor(t, x, y, ALU.mult))
                link(dve.tensor_tensor(t, t, y, ALU.mult))
                link(dve.tensor_scalar(t, t, -0.5, 1.5, ALU.mult, ALU.add))
                return dve.tensor_tensor(y, y, t, ALU.mult)

            def job_read(i, k, unit):
                dve.wait_ge(on["units_multiplied"], unit.upto(-1))
                out = bank((J_PROJECT + k) % 2, 0, T)
                if k == 0:
                    dve.wait_ge(on["decay_ready"], i * 3 + 1)
                    last = dve.scalar_tensor_tensor(out=q_dec, in0=out, scalar=DK ** -0.5, in1=decay, op0=ALU.mult, op1=ALU.mult)
                elif k == 1:
                    dve.wait_ge(on["decay_ready"], i * 3 + 3)
                    link(dve.tensor_tensor(k_inv, out, k_inv, ALU.mult))
                    last = dve.tensor_tensor(k_end_f, out, k_end_f, ALU.mult)
                elif k < 4:
                    last = dve.tensor_copy(v_f[:, k - 2, :], out)
                elif k < 6:
                    dve.wait_ge(on["swish_exp_ready"], i * 2 + (k - 3))
                    r = silu_r[:, k - 4, :]
                    link(dve.tensor_scalar(r, r, 1.0, None, ALU.add))
                    link(dve.reciprocal(r, r))
                    last = dve.tensor_tensor(r, out, r, ALU.mult)
                elif k < 12:
                    j, n = (k - 6) // 3, (k - 6) % 3
                    if n == 0:
                        last = dve.tensor_scalar(fox_qkv[:, j, n, :], out, DH ** -0.5, None, ALU.mult)
                    else:
                        last = dve.tensor_copy(fox_qkv[:, j, n, :], out)
                else:
                    last = dve.tensor_copy(gates[:, ds(i * 8 + (k - 12), 1), :].rearrange("p o t -> p (o t)"), out)
                last.then_inc(on["jobs_read"], 1)

            def gla(i, s):
                if s == 10:
                    dve.wait_ge(on["gla_v_ready"], i * 4 + 4)
                    for b0, out in ((0, k_end_early), (NB // 2, k_end_late)):
                        dve.tensor_tensor(out, bank(4, DV, DK, CH).unsqueeze(1).to_broadcast([CH, NB // 2, DK]),
                                                 own_rows[:, b0:b0 + NB // 2].unsqueeze(2).to_broadcast([CH, NB // 2, DK]),
                                                 ALU.mult)
                    dve.copy_predicated(attn_gla[:, :, :], keep_gla[:, :, :], bank3(6, 0, NC + 1, CH, CH)
                                        ).then_inc(on["gla_attn_ready"], 1)
                if s == 12:
                    dve.wait_ge(on["gla_intra_done"], i + 1)
                    link(dve.tensor_copy(states[:, 0, :], bank(2, 0, DV)))
                    for c in range(1, NC):
                        end = c * CH + CH - 1
                        step = dve.scalar_tensor_tensor(out=states[:, c, :], in0=states[:, c - 1, :], scalar=decay[:, end:end + 1],
                                                        in1=bank(2 + c // 2, (c % 2) * DV, DV), op0=ALU.mult, op1=ALU.add)
                        if c < NC - 1:
                            link(step)
                    step.then_inc(on["gla_states_ready"], 1)
                    for b in range(NB // 2):
                        sample_state(b, 4 + b // 2)
                if s == 15:
                    dve.wait_ge(on["gla_inter_done"], i + 1)
                    for b in range(NB // 2, NB):
                        last = sample_state(b, 2 + (b - NB // 2) // 2)
                    last.then_inc(on["gla_states_s_ready"], 1)
                    dve.wait_ge(on["gla_squares"], i * 2 + 2)
                    dve.tensor_tensor(k_inv, squares[:, 0, :], squares[:, 1, :], ALU.add).then_inc(on["gla_sum_ready"], 1)
                if s == 17:
                    dve.wait_ge(on["gla_sum_spread"], i + 1)
                    dve.tensor_scalar(k_end_f, bank(5, 0, T), 1.0 / DV, EPS, ALU.mult, ALU.add).then_inc(on["gla_mean_ready"], 1)
                if s == 18:
                    dve.wait_ge(on["gla_rstd_rough"], i + 1)
                    link(refine(decay, k_end_f, k_inv))
                    for j in range(VT):
                        link(dve.tensor_tensor(o_gla[:, j, :], bank(7 - j, 0, T), decay, ALU.mult))
                        last = dve.scalar_tensor_tensor(out=o_gla[:, j, :], in0=o_gla[:, j, :],
                                                        scalar=gains[:, ds(i * 2 + (G_GLA + j), 1)], in1=silu_r[:, j, :],
                                                        op0=ALU.mult, op1=ALU.mult)
                        if j < VT - 1:
                            link(last)
                    last.then_inc(on["gla_out_ready"], 1)
                if s == 19:
                    dve.wait_ge(on["gla_high_ready"], i + 1)
                    dve.tensor_tensor(b_low[:, ds(i * 2, 2), :], o_gla, b_high[:, ds(i * 2, 2), :].bitcast(F32), ALU.subtract
                                      ).then_inc(on["gla_low_ready"], 1)

            def sample_state(b, at):
                end = SEQ + b * NT + NT - 1
                return dve.scalar_tensor_tensor(out=states_s[:, b, :], in0=states_s[:, b, :], scalar=decay[:, end:end + 1],
                                                in1=bank(at, (b % 2) * DV, DV), op0=ALU.mult, op1=ALU.add)

            def fox(i, j, step):
                n = i * 2 + (j + 1)
                head = ds(i * 2 + j, 1)
                if step == 0:
                    past = lf_past[:, :, head].rearrange("p (b g) o -> p g (b o)", g=PAGES)
                    dve.tensor_copy(lf_wide.rearrange("p g (b t) -> p g b t", t=NT),
                                    past.unsqueeze(3).to_broadcast([P, PAGES, NB, NT]))
                    dve.tensor_scalar(neg_c, c_rows[:, :], minus_head[:, head], None, ALU.mult).then_inc(on["fox_rows_ready"], 1)
                if step == 1:
                    dve.wait_ge(on["fox_logits_done"], n)
                    c0, c1 = (c_tok[:, k, head] for k in range(2))
                    dve.scalar_tensor_tensor(out=probs[:, 0:P], in0=bank(4, 0, P), scalar=c0, in1=causal[:, :],
                                             op0=ALU.add, op1=ALU.add)
                    dve.tensor_scalar(probs[:, P:2 * P], bank(4, P, P), c1, None, ALU.add)
                    link(dve.scalar_tensor_tensor(out=probs[:, 2 * P:3 * P], in0=bank(4, 2 * P, P), scalar=c1, in1=causal[:, :],
                                                  op0=ALU.add, op1=ALU.add))
                    dve.tensor_reduce(out=stat[:, 6:7], in_=probs[:, 0:P], axis=AX, op=ALU.max, negate=True)
                    dve.tensor_reduce(out=stat[:, 7:8], in_=probs[:, P:3 * P], axis=AX, op=ALU.max, negate=True
                                      ).then_inc(on["fox_max_ready"], 1)
                if step == 2:
                    dve.wait_ge(on["fox_exp_ready"], n * 2)
                    link(dve.reciprocal(stat[:, 12:14], stat[:, 8:10]))
                    dve.tensor_scalar(probs[:, 0:P], probs[:, 0:P], stat[:, 12:13], None, ALU.mult)
                    dve.tensor_scalar(probs[:, P:3 * P], probs[:, P:3 * P], stat[:, 13:14], None, ALU.mult
                                      ).then_inc(on["fox_probs_ready"], 1)
                if step == 3:
                    dve.wait_ge(on["fox_qk_done"], n)
                    dve.tensor_copy(scores_t, bank3(2, 3 * P, PAGES, SAMPLE)).then_inc(on["fox_scores_t_ready"], 1)
                if step == 4:
                    dve.wait_ge(on["fox_rows_done"], n)
                    c2 = c_tok[0:SAMPLE, 2, head]
                    dve.tensor_scalar(probs_s[:, 0:2 * P], bank(5, 0, 2 * P, SAMPLE), c2, None, ALU.add)
                    link(dve.scalar_tensor_tensor(out=probs_s[:, 2 * P:2 * P + SAMPLE], in0=bank(5, 2 * P, SAMPLE, SAMPLE), scalar=c2,
                                                  in1=causal_s[:, :], op0=ALU.add, op1=ALU.add))
                    dve.tensor_reduce(out=stat[0:SAMPLE, 10:11], in_=probs_s, axis=AX, op=ALU.max, negate=True
                                      ).then_inc(on["fox_max_s_ready"], 1)
                if step == 5:
                    dve.wait_ge(on["fox_exp_s_ready"], n)
                    link(dve.reciprocal(stat[0:SAMPLE, 14:15], stat[0:SAMPLE, 11:12]))
                    dve.tensor_scalar(probs_s, probs_s, stat[0:SAMPLE, 14:15], None, ALU.mult).then_inc(on["fox_probs_s_ready"], 1)
                if step == 7:
                    dve.wait_ge(on["fox_high_ready"], n)
                    out = ds(i * 2 + (KT // 2 + j), 1)
                    dve.tensor_tensor(b_low[:, out, :].rearrange("p o t -> p (o t)"), bank(3, 0, T),
                                      b_high[:, out, :].rearrange("p o t -> p (o t)").bitcast(F32), ALU.subtract
                                      ).then_inc(on["fox_out_read"], 1)

            dve.memset(raw[:, 0:2, :], 0.0).then_inc(on["narrow_cleared"], 1)
            dve.sem_inc(on["low_ready"], HEAD)
            for name in ("jobs_read", "fox_out_read", "merged_ready"):
                dve.sem_inc(on[name], START)
            link(dve.memset(stat[:, :], 1.0))
            link(dve.memset(attn_gla[:, :, :], 0.0))
            dve.sem_inc(on["stat_cleared"], 1)

            dve.wait_ge(on["x_squared"], 3)
            link(dve.tensor_scalar(stat[:, 0:3], stat[:, 0:3], 1.0 / D, EPS, ALU.mult, ALU.add))
            dve.sem_inc(on["x_mean_ready"], 1)
            dve.wait_ge(on["x_rstd_rough"], 1)
            link(refine(stat[:, 3:6], stat[:, 0:3], stat[:, 6:9]))
            for k in range(3):
                rows = P if k < 2 else SAMPLE
                dve.tensor_scalar(x_tok[0:rows, k, :], x_tok[0:rows, k, :], stat[0:rows, 3 + k:4 + k], None, ALU.mult
                                  ).then_inc(on["x_scaled"], 1)
            dve.wait_ge(on["gains_turned"], 1)
            dve.tensor_copy(gains[:, :], bank(7, 0, 60)).then_inc(on["gains_ready"], 1)
            dve.wait_ge(on["gains_ready"], 1)
            prepare(Unit(0))
            prepare(Unit(1))
            for m in range(KT):
                dve.wait_ge(on["x_high_ready"], m + 1)
                dve.scalar_tensor_tensor(out=a_low[:, m, :], in0=bank(2 + m % 4, 0, T), scalar=gains[:, G_ATTN + m:G_ATTN + m + 1],
                                         in1=a_high[:, m, :].bitcast(F32), op0=ALU.mult, op1=ALU.subtract
                                         ).then_inc(on["x_low_ready"], 1)
            prepare(Unit(2))
            prepare(Unit(3))

            dve.wait_ge(on["units_multiplied"], 2)
            dve.wait_ge(on["a2_landed"], 32)
            link(dve.tensor_copy(ga1, psum[32:32 + RANK, 0, 0:T]))
            link(dve.tensor_scalar(z_row, bank(0, 0, T, FH), bias_ff[:, 0:1], None, ALU.add))
            dve.sem_inc(on["jobs_read"], 1)
            dve.sem_inc(on["ga1_ready"], 1)
            dve.sem_inc(on["z_row_ready"], 1)
            dve.wait_ge(on["e_row_ready"], 1)
            link(dve.scalar_tensor_tensor(out=lf_rows, in0=z_row, scalar=0.0, in1=e_row, op0=ALU.min, op1=ALU.subtract))
            dve.wait_ge(on["constants_ready"], 1)
            dve.tensor_tensor_scan(c_rows[:, :], scan_fox, lf_rows, 0.0, ALU.mult, ALU.add).then_inc(on["c_rows_ready"], 1)
            for h in range(GH):
                dve.wait_ge(on["a2_multiplied"], h + 1)
                dve.tensor_scalar(z_all[:, h, :], bank(2 + h, 0, T), gains[:, B_GLA + h:B_GLA + h + 1], None, ALU.add
                                  ).then_inc(on["z_all_ready"], 1)
            dve.wait_ge(on["c_turned"], 1)
            for k in range(3):
                rows = P if k < 2 else SAMPLE
                link(dve.tensor_copy(c_tok[0:rows, k, :], bank(6, 8 * k, FH, rows)))
                link(dve.tensor_copy(lf_tok[0:rows, k, :], bank(6, 32 + 8 * k, FH, rows)))
            dve.sem_inc(on["lf_tok_ready"], 1)
            for h in range(GH):
                dve.wait_ge(on["e_all_ready"], h + 1)
                link(dve.scalar_tensor_tensor(out=z_all[:, h, :], in0=z_all[:, h, :], scalar=0.0, in1=e_all[:, h, :],
                                              op0=ALU.min, op1=ALU.subtract))
                link(dve.tensor_scalar(z_all[:, h, :], z_all[:, h, :], 1.0 / 16.0, None, ALU.mult))
                link(dve.tensor_tensor_scan(decay_all[:, h, :], scan_gla, z_all[:, h, :], 0.0, ALU.mult, ALU.add))
            dve.wait_ge(on["lf_past_landed"], 16 * NB * PAGES)
            dve.wait_ge(on["lf_stored"], 32)
            dve.sem_inc(on["start_done"], 1)

            with dve.Fori(0, TURNS) as i:
                own.enter(i, VECTOR_STEPS["project"])
                for s in range(2 * JOBS):
                    unit = Unit(U_PROJECT + s, i * (2 * JOBS // SLOTS))
                    prepare(unit.plus(LEAD))
                    if s == 0:
                        dve.wait_ge(on["kv_stored"], i * 128 + START)
                        b = decay_all[:, ds(i, 1), :].rearrange("p o t -> p (o t)")
                        for a, n, t in ((0, NC, CH), (SEQ, NB, NT)):
                            bv = decay_all[:, ds(i, 1), a:a + n * t].rearrange("p o (c t) -> p (o c) t", t=t)
                            link(dve.tensor_tensor(k_end_f[:, a:a + n * t].rearrange("p (c t) -> p c t", t=t),
                                                   bv[:, :, t - 1:t].to_broadcast([P, n, t]), bv, ALU.subtract))
                        dve.sem_inc(on["to_end_ready"], 1)
                    if s >= 2 and s % 2 == 0:
                        job_read(i, s // 2 - 1, unit)
                    gla(i, s)
                    for j, at in enumerate(FOX_AT):
                        fox(i, j, s - at)
                job_read(i, JOBS - 1, Unit(U_PROJECT + 2 * JOBS, i * (2 * JOBS // SLOTS)))
                own.leave(TURNS, "vector, projection")

            with dve.Fori(0, KT // 4) as i:
                own.enter(i, VECTOR_STEPS["merge"])
                for r in range(4):
                    prepare(Unit(U_MERGE + 2 * r, i * 2).plus(LEAD))
                    unit = Unit(U_MERGE + 2 * r + 1, i * 2)
                    prepare(unit.plus(LEAD))
                    dve.wait_ge(on["sig_ready"], i * 4 + (r + 1))
                    dve.wait_ge(on["units_multiplied"], unit.upto(-1))
                    link(dve.tensor_tensor(prod_a, bank(J_MERGE % 2, 0, T), sig[:, 0, :], ALU.mult))
                    dve.sem_inc(on["jobs_read"], 1)
                    dve.wait_ge(on["units_multiplied"], unit.upto())
                    dve.tensor_tensor(prod_b, bank((J_MERGE + 1) % 2, 0, T), sig[:, 1, :], ALU.mult).then_inc(on["jobs_read"], 1)
                    dve.wait_ge(on["jobs_read"], i * 8 + (J_MERGE + 2 * r + 2 + START))
                    dve.tensor_tensor(merged, prod_a, prod_b, ALU.add).then_inc(on["merged_ready"], 1)
                    dve.wait_ge(on["merged_high_ready"], i * 4 + (r + 1))
                    m = i * 4 + r
                    dve.tensor_tensor(a_low[:, ds(m, 1), :].rearrange("p o t -> p (o t)"), merged,
                                      a_high[:, ds(m, 1), :].rearrange("p o t -> p (o t)").bitcast(F32), ALU.subtract
                                      ).then_inc(on["merged_low_ready"], 1)
                own.leave(KT // 4, "vector, merge")

            link(dve.memset(sum_sq, 0.0))
            with dve.Fori(0, KT // 2) as i:
                own.enter(i, VECTOR_STEPS["out"])
                for r in range(2):
                    prepare(Unit(U_OUT + 2 * r, i).plus(LEAD))
                    unit = Unit(U_OUT + 2 * r + 1, i)
                    prepare(unit.plus(LEAD))
                    m = i * 2 + r
                    x2 = resid[:, ds(m, 1), :].rearrange("p o t -> p (o t)")
                    dve.wait_ge(on["units_multiplied"], unit.upto())
                    link(dve.tensor_copy(x2, bank((J_OUT + r) % 2, 0, T)))
                    dve.sem_inc(on["jobs_read"], 1)
                    dve.sem_inc(on["resid_ready"], 1)
                    dve.tensor_scalar(scaled, x2, gains[:, ds(m + G_FFN, 1)], None, ALU.mult).then_inc(on["scaled_ready"], 1)
                    dve.wait_ge(on["square_ready"], m + 1)
                    link(dve.tensor_tensor(sum_sq, sum_sq, square, ALU.add))
                    dve.wait_ge(on["scaled_high_ready"], m + 1)
                    dve.tensor_tensor(b_low[:, ds(m, 1), :].rearrange("p o t -> p (o t)"), scaled,
                                      b_high[:, ds(m, 1), :].rearrange("p o t -> p (o t)").bitcast(F32), ALU.subtract
                                      ).then_inc(on["scaled_low_ready"], 1)
                own.leave(KT // 2, "vector, output projection")
            dve.sem_inc(on["sum_ready"], 1)
            dve.wait_ge(on["kv_stored"], 64 * FH + START)
            dve.wait_ge(on["sum_spread"], 1)
            link(dve.tensor_scalar(mean, bank(2, 0, T), 1.0 / D, EPS, ALU.mult, ALU.add))
            dve.sem_inc(on["ffn_mean_ready"], 1)
            dve.wait_ge(on["ffn_rstd_rough"], 1)
            link(refine(rstd, mean, rtmp))
            link(dve.memset(sum_sq, 0.0))

            def chunk(c, final):
                def gate_up(f, last):
                    unit = Unit(U_FFN, c * (U_CHUNK // 4) + f)
                    for s in range(4):
                        prepare(unit.plus(s + LEAD), (6, 5)[s % 2] if last and s >= 2 else UNIT)
                        if s == 2:
                            dve.wait_ge(on["units_multiplied"], unit.upto(1))
                            link(dve.tensor_tensor(gate_s, bank(J_FFN % 2, 0, T), rstd, ALU.mult))
                            dve.sem_inc(on["jobs_read"], 1)
                            dve.sem_inc(on["gate_ready"], 1)
                    dve.wait_ge(on["units_multiplied"], unit.upto(3))
                    link(dve.tensor_tensor(up_s, bank((J_FFN + 1) % 2, 0, T), rstd, ALU.mult))
                    dve.sem_inc(on["jobs_read"], 1)
                    dve.wait_ge(on["silu_ready"], c * CT + f + 1)
                    dve.tensor_tensor(hidden, silu_g, up_s, ALU.mult).then_inc(on["hidden_ready"], 1)
                    dve.wait_ge(on["hidden_high_ready"], c * CT + f + 1)
                    dve.tensor_tensor(a_low[:, ds(f, 1), :].rearrange("p o t -> p (o t)"), hidden,
                                      a_high[:, ds(f, 1), :].rearrange("p o t -> p (o t)").bitcast(F32), ALU.subtract
                                      ).then_inc(on["hidden_low_ready"], 1)

                with dve.Fori(0, CT - 1) as f:
                    own.enter(f, VECTOR_STEPS["gate"])
                    gate_up(f, False)
                    own.leave(CT - 1, "vector, gate and up")
                gate_up(CT - 1, True)

                def down(m, last):
                    unit = Unit(U_FFN + 4 * CT, c * (U_CHUNK // 4) + m)
                    for r in range(2):
                        for s in (2 * r, 2 * r + 1):
                            if not last or s < 2:
                                prepare(unit.plus(s + LEAD), (6, 5)[s % 2])
                            elif not final:
                                prepare(unit.plus(s + LEAD), UNIT)
                        x2 = resid[:, ds(m * 2 + r, 1), :].rearrange("p o t -> p (o t)")
                        dve.wait_ge(on["units_multiplied"], unit.plus(2 * r + 1).upto())
                        link(dve.tensor_tensor(x2, bank((J_FFN + r) % 2, 0, T), x2, ALU.add))
                        dve.sem_inc(on["jobs_read"], 1)
                        if final:
                            dve.sem_inc(on["resid_final"], 1)
                            dve.wait_ge(on["y_turned"], m * 2 + START)
                            dve.tensor_scalar(y_feat[:, r, :], x2, gains[:, ds(m * 2 + (G_FINAL + r), 1)], None, ALU.mult
                                              ).then_inc(on["y_feat_ready"], 1)
                            dve.wait_ge(on["square_ready"], m * 2 + (KT + r + 1))
                            link(dve.tensor_tensor(sum_sq, sum_sq, square, ALU.add))

                with dve.Fori(0, KT // 2 - 1) as m:
                    own.enter(m, VECTOR_STEPS["down_final" if final else "down"])
                    down(m, False)
                    own.leave(KT // 2 - 1, "vector, down")
                down(KT // 2 - 1, True)

            with dve.Fori(0, CHUNKS - 1) as c:
                own.enter(c, VECTOR_STEPS["chunk"])
                chunk(c, False)
                own.leave(CHUNKS - 1, "vector, chunk")
            chunk(CHUNKS - 1, True)

            dve.sem_inc(on["sum_ready"], 1)
            dve.wait_ge(on["sum_by_token"], 1)
            for k in range(3):
                rows = P if k < 2 else SAMPLE
                link(dve.tensor_scalar(stat[0:rows, k:k + 1], bank(6, k, 1, rows), 1.0 / D, EPS, ALU.mult, ALU.add))
            dve.sem_inc(on["y_mean_ready"], 1)
            dve.wait_ge(on["y_rstd_rough"], 1)
            link(refine(stat[:, 3:6], stat[:, 0:3], stat[:, 6:9]))
            dve.sem_inc(on["y_rstd_ready"], 1)
            dve.wait_ge(on["y_copied"], 2 * KT + START)
            dve.tensor_scalar(y_tok[:, 0, :], y_tok[:, 0, :], stat[:, 3:4], None, ALU.mult).then_inc(on["y_scaled_0"], 1)
            dve.tensor_scalar(y_tok_s, y_tok_s, stat[0:SAMPLE, 5:6], None, ALU.mult
                              ).then_inc(on["y_scaled_2"], 1)

        @block.tensor
        def _(pe):
            def multiply(unit, tiles, x_high, x_low, b, first, last, ready=None):
                pe.wait_ge(on["low_ready"], unit.upto(HEAD))
                for n, k in enumerate(tiles):
                    if ready:
                        ready(k)
                    w_high = high[:, unit.slot, n * P:(n + 1) * P]
                    w_low = low[:, unit.slot, n * P:(n + 1) * P]
                    end = last and n == len(tiles) - 1
                    pe.matmul(bank(b, 0, T), w_high, x_high[:, k, :], start=first and n == 0, stop=False,
                              skip_group_check=True)
                    pe.matmul(bank(b, 0, T), w_high, x_low[:, k, :], start=False, stop=False, skip_group_check=True)
                    done = pe.matmul(bank(b, 0, T), w_low, x_high[:, k, :], start=False, stop=end, skip_group_check=True)
                done.then_inc(on["units_multiplied"], 1)

            def turn(out, in_, rows):
                return pe.transpose(out, in_, ident[0:rows, 0:rows])

            def add(out, lhsT, rhs, start=False, stop=False):
                return pe.matmul(out, lhsT, rhs, start=start, stop=stop, skip_group_check=True)

            for name in ("fox_pv_done", "y_turned"):
                pe.sem_inc(on[name], START)
            pe.wait_ge(on["ident_ready"], 1)
            pe.wait_ge(on["gains_landed"], 80)
            turn(bank(7, 0, 60), g_rows, 60).then_inc(on["gains_turned"], 1)
            pe.wait_ge(on["x_scaled"], 3)
            for m in range(KT):
                if m >= 4:
                    pe.wait_ge(on["x_low_ready"], m - 3)
                for k in range(3):
                    rows = P if k < 2 else SAMPLE
                    last = turn(bank(2 + m % 4, k * P, rows), x_tok[0:rows, k, m * P:(m + 1) * P], rows)
                last.then_inc(on["x_turned"], 1)
            for u in range(2):
                multiply(Unit(u), range(u * UNIT, (u + 1) * UNIT), a_high, a_low, 0, u == 0, u == 1,
                         ready=lambda k: pe.wait_ge(on["x_low_ready"], k + 1))
            pe.wait_ge(on["ga1_ready"], 1)
            for h in range(GH):
                pe.matmul(bank(2 + h, 0, T), w_a2[:, h * DK:(h + 1) * DK], ga1, start=True, stop=True
                          ).then_inc(on["a2_multiplied"], 1)
            pe.wait_ge(on["c_rows_ready"], 1)
            for k in range(3):
                rows = P if k < 2 else SAMPLE
                turn(bank(6, 8 * k, FH, rows), c_rows[:, k * P:k * P + rows], FH)
                last = turn(bank(6, 32 + 8 * k, FH, rows), lf_rows[:, k * P:k * P + rows], FH)
            last.then_inc(on["c_turned"], 1)
            pe.wait_ge(on["constants_ready"], 1)

            def gla(i, step):
                if step == 1:
                    pe.wait_ge(on["jobs_read"], i * JOBS + (J_PROJECT + 4 + START))
                    pe.wait_ge(on["fox_out_read"], i * 2 + START)
                    for c in range(NC + 1):
                        cols = slice(c * CH, (c + 1) * CH)
                        pe.matmul(bank(6, c * CH, CH, CH), k_inv[:, cols], q_dec[:, cols], start=True, stop=True)
                    for c in range(NC + 1):
                        cols = slice(c * CH, (c + 1) * CH)
                        for j in range(VT):
                            turn(bank(2 + c // 2, (c % 2) * DV + j * P, P, CH), v_f[:, j, cols], P)
                        if c < NC:
                            last = turn(bank(5, c * DK, DK, CH), k_end_f[:, cols], P)
                        else:
                            last = turn(bank(4, DV, DK, CH), k_end_f[:, cols], P)
                    last.then_inc(on["gla_turned"], 1)
                if step == 2:
                    pe.wait_ge(on["gla_v_ready"], i * 4 + 4)
                    pe.wait_ge(on["gla_attn_ready"], i + 1)
                    pe.wait_ge(on["states_landed"], i * 16 + 16)
                    for c in range(NC):
                        last = pe.matmul(bank(2 + c // 2, (c % 2) * DV, DV), k_end[:, c, :], gla_v[:, c, :],
                                         start=True, stop=True)
                    for j in range(VT):
                        for c in range(NC + 1):
                            add(bank(7 - j, c * CH, CH), gla_v[:, c, j * P:(j + 1) * P], attn_gla[:, c, :], start=c == 0)
                        for b in range(NB):
                            add(bank(7 - j, SEQ + b * NT, NT), states_s[:, b, j * P:(j + 1) * P],
                                q_dec[:, SEQ + b * NT:SEQ + (b + 1) * NT])
                    for b in range(NB // 2):
                        last = pe.matmul(bank(4 + b // 2, (b % 2) * DV, DV), k_end_early[:, b, :], gla_v[:, NC, :],
                                         start=True, stop=True)
                    last.then_inc(on["gla_intra_done"], 1)
                if step == 3:
                    pe.wait_ge(on["gla_states_ready"], i + 1)
                    for j in range(VT):
                        for c in range(1, NC):
                            add(bank(7 - j, c * CH, CH), states[:, c - 1, j * P:(j + 1) * P],
                                q_dec[:, c * CH:(c + 1) * CH], stop=c == NC - 1)
                    for b in range(NB // 2):
                        last = pe.matmul(bank(2 + b // 2, (b % 2) * DV, DV), k_end_late[:, b, :], gla_v[:, NC, :],
                                         start=True, stop=True)
                    last.then_inc(on["gla_inter_done"], 1)
                if step == 4:
                    pe.wait_ge(on["gla_sum_ready"], i + 1)
                    pe.matmul(bank(5, 0, T), ones[:, :], k_inv, start=True, stop=True).then_inc(on["gla_sum_spread"], 1)

            def fox(i, j, step):
                q, k, v = (fox_qkv[:, j, n, :] for n in range(3))
                n = i * 2 + (j + 1)
                if step == 0:
                    pe.wait_ge(on["jobs_read"], i * JOBS + (J_PROJECT + 9 + 3 * j + START))
                    pe.wait_ge(on["fox_rows_ready"], n)
                    if j == 0:
                        pe.wait_ge(on["gla_out_ready"], i + 1)
                        pe.wait_ge(on["gla_high_ready"], i + 1)
                    else:
                        pe.wait_ge(on["fox_out_read"], n - 1 + START)
                    for b, x in ((2, k), (3, v)):
                        for t in range(3):
                            rows = P if t < 2 else SAMPLE
                            turn(bank(b, t * DH, DH, rows), x[:, t * P:t * P + rows], P)
                    for cols, queries, nk in ((0, slice(0, P), P), (P, slice(P, 2 * P), 2 * P)):
                        add(bank(4, cols, nk), q[:, queries], k[:, 0:nk], start=True)
                        add(bank(4, cols, nk), ones[0:FH, :], neg_c[:, 0:nk], stop=True)
                    rows = bank(5, 0, 5 * SAMPLE, SAMPLE)
                    add(rows[:, 2 * P:2 * P + SAMPLE], q[:, SEQ:T], k[:, SEQ:T], start=True)
                    add(rows[:, 2 * P:2 * P + SAMPLE], ones[0:FH, 0:SAMPLE], neg_c[:, SEQ:T])
                    add(rows[:, 0:P], lf_wide[:, 0, :], later[:, :])
                    add(rows[:, 0:P], lf_wide[:, 1, :], ones[:, :])
                    add(rows[:, P:2 * P], lf_wide[:, 1, :], later[:, :]).then_inc(on["fox_logits_done"], 1)
                    turn_keys(n, 0)
                if step == 1:
                    turn_keys(n, 1)
                    past_logits(n, 0)
                if step == 2:
                    past_logits(n, 1)
                if step == 3:
                    pe.wait_ge(on["fox_scores_t_ready"], n)
                    for g in range(PAGES):
                        last = add(bank(5, g * P, P, SAMPLE), scores_t[:, g, :], ident[:, :], stop=g == 1)
                    last.then_inc(on["fox_rows_done"], 1)
                    pe.wait_ge(on["fox_probs_ready"], n)
                    for b in range(3):
                        last = turn(bank(4, b * P, P), probs[:, b * P:(b + 1) * P], P)
                    last.then_inc(on["fox_probs_turned"], 1)
                if step == 4:
                    pe.wait_ge(on["fox_probs_t_ready"], n)
                    add(bank(3, 0, P), v_tok[:, 0, :], probs_t[:, 0, :], start=True, stop=True)
                    add(bank(3, P, P), v_tok[:, 0, :], probs_t[:, 1, :], start=True)
                    add(bank(3, P, P), v_tok[:, 1, :], probs_t[:, 2, :], stop=True)
                if step == 5:
                    pe.wait_ge(on["fox_probs_s_ready"], n)
                    for g in range(PAGES):
                        pe.matmul(bank(4, g * SAMPLE, SAMPLE), probs_s[:, g * P:(g + 1) * P], ident[0:SAMPLE, 0:SAMPLE],
                                  start=True, stop=True)
                    turn(bank(4, 2 * SAMPLE, SAMPLE, SAMPLE), probs_s[:, 2 * P:2 * P + SAMPLE], SAMPLE
                         ).then_inc(on["fox_probs_s_turned"], 1)
                if step == 6:
                    pe.wait_ge(on["fox_probs_st_ready"], n * 2)
                    pe.wait_ge(on["values_landed"], n * (16 * NB * PAGES))
                    add(bank(3, SEQ, SAMPLE), v_tok[0:SAMPLE, 2, :], probs_st[0:SAMPLE, 2, :], start=True)
                    for b in range(NB):
                        for g in range(PAGES):
                            last = add(bank(3, SEQ + b * NT, NT), values[:, PAGES * b + g, :],
                                       probs_st[:, g, b * NT:(b + 1) * NT], stop=g == 1)
                    last.then_inc(on["fox_pv_done"], 1)

            def turn_keys(n, half):
                if half == 0:
                    pe.wait_ge(on["keys_landed"], n * (16 * NB * PAGES))
                else:
                    pe.wait_ge(on["fox_keys_ready"], n * 4 - 2)
                for r in range(8):
                    last = turn(bank(6 + r // 4, (r % 4) * DH, DH), keys[:, 8 * half + r, :], P)
                last.then_inc(on["fox_keys_turned"], 1)

            def past_logits(n, half):
                if half == 0:
                    pe.wait_ge(on["fox_tokens_ready"], n)
                else:
                    pe.wait_ge(on["fox_keys_ready"], n * 4)
                q = fox_q[0]
                for r in range(8):
                    b, g = (8 * half + r) // PAGES, r % PAGES
                    last = pe.matmul(bank(2, 3 * P + g * SAMPLE + b * NT, NT), keys[:, PAGES * b + g, :],
                                     q[:, SEQ + b * NT:SEQ + (b + 1) * NT], start=True, stop=True)
                if half == 1:
                    last.then_inc(on["fox_qk_done"], 1)

            fox_q = [None]
            with pe.Fori(0, TURNS) as i:
                for s in range(2 * JOBS):
                    job = J_PROJECT + s // 2
                    unit = Unit(U_PROJECT + s, i * (2 * JOBS // SLOTS))
                    if s % 2 == 0 :
                        pe.wait_ge(on["jobs_read"], i * JOBS + (job - 1 + START))
                    multiply(unit, range((s % 2) * UNIT, (s % 2 + 1) * UNIT), a_high, a_low, job % 2, s % 2 == 0, s % 2 == 1)
                    if s in (8, 11, 13, 16):
                        gla(i, (8, 11, 13, 16).index(s) + 1)
                    for j, at in enumerate(FOX_AT):
                        if 0 <= s - at < 7:
                            fox_q[0] = fox_qkv[:, j, 0, :]
                            fox(i, j, s - at)

            pe.wait_ge(on["start_done"], 1)
            pe.wait_ge(on["gla_low_ready"], TURNS)
            pe.wait_ge(on["fox_out_read"], FH + START)
            with pe.Fori(0, KT // 4) as i:
                for s in range(8):
                    job = J_MERGE + s
                    pe.wait_ge(on["jobs_read"], i * 8 + (job - 1 + START))
                    multiply(Unit(U_MERGE + s, i * 2), range((s % 2) * 8, (s % 2) * 8 + 8), b_high, b_low, job % 2, True, True)

            pe.sem_inc(on["slabs_used"], START + 1)
            with pe.Fori(0, KT // 2) as i:
                for r in range(2):
                    job = J_OUT + r
                    b = job % 2
                    pe.wait_ge(on["jobs_read"], i * 2 + (job - 1 + START))
                    pe.wait_ge(on[f"slab_landed_{r}"], i * 32 + 32)
                    for t in range(3):
                        rows = P if t < 2 else SAMPLE
                        last = add(bank(b, t * P, rows), x_slab[0:rows, r, t, :], ident[0:rows, 0:rows], start=t == 0)
                    last.then_inc(on["slabs_used"], 1)
                    for s in (2 * r, 2 * r + 1):
                        multiply(Unit(U_OUT + s, i), range((s % 2) * UNIT, (s % 2 + 1) * UNIT), a_high, a_low, b, False, s % 2 == 1,
                                 ready=lambda k: pe.wait_ge(on["merged_low_ready"], k + 1))

            pe.wait_ge(on["sum_ready"], 1)
            pe.matmul(bank(2, 0, T), ones[:, :], sum_sq, start=True, stop=True).then_inc(on["sum_spread"], 1)
            pe.wait_ge(on["scaled_low_ready"], KT)

            def chunk(c, final):
                with pe.Fori(0, CT) as f:
                    for s in range(4):
                        job = J_FFN + s // 2
                        if s % 2 == 0:
                            pe.wait_ge(on["jobs_read"], c * J_CHUNK + f * 2 + (job - 1 + START))
                        multiply(Unit(U_FFN + s, c * (U_CHUNK // 4) + f), range((s % 2) * UNIT, (s % 2 + 1) * UNIT),
                                 b_high, b_low, job % 2, s % 2 == 0, s % 2 == 1,
                                 )

                def y_turn(r, n):
                    pe.wait_ge(on["y_feat_ready"], n)
                    for t in range(3):
                        rows = P if t < 2 else SAMPLE
                        last = turn(bank(2 + r, t * P, P, rows), y_feat[:, r, t * P:t * P + rows], P)
                    last.then_inc(on["y_turned"], 1)

                def down(m, first):
                    for r in range(2):
                        job = J_FFN + 2 * CT + r
                        pe.wait_ge(on["jobs_read"], c * J_CHUNK + m * 2 + (job - 1 + START))
                        for s, (a, n) in enumerate(((0, 6), (6, 5))):
                            multiply(Unit(U_FFN + 4 * CT + 2 * r + s, c * (U_CHUNK // 4) + m), range(a, a + n), a_high, a_low,
                                     job % 2, s == 0, s == 1,
                                     ready=lambda k: pe.wait_ge(on["hidden_low_ready"], c * CT + (k + 1)))
                        if final and (r == 1 or not first):
                            if not first:
                                pe.wait_ge(on["y_copied"], m * 4 + (2 * r - 4 + START))
                            y_turn(1 - r, m * 2 + r)

                down(0, True)
                with pe.Fori(1, KT // 2) as m:
                    down(m, False)
                if final:
                    pe.wait_ge(on["y_copied"], 2 * (KT - 2) + START)
                    y_turn(1, KT)

            with pe.Fori(0, CHUNKS - 1) as c:
                chunk(c, False)
            chunk(CHUNKS - 1, True)
            pe.wait_ge(on["sum_ready"], 2)
            for t in range(3):
                rows = P if t < 2 else SAMPLE
                last = pe.matmul(bank(6, t, 1, rows), sum_sq[:, t * P:t * P + rows], ones[:, 0:1], start=True, stop=True)
            last.then_inc(on["sum_by_token"], 1)


_INS = ["x_prompt", "x_sample", "cache_k", "cache_v", "cache_lf", "state_gla", "page_table", "g_attn", "w_in", "w_gla_a2",
        "b_gla_a", "b_fox_f", "g_gla_norm", "w_pa", "w_pb", "w_o", "g_ffn", "w_gate", "w_up", "w_down", "g_final"]


def kernel(**inputs):
    import numpy as np
    import concourse.bacc as bacc
    from concourse.bass_utils import run_bass_kernel_spmd

    nc = bacc.Bacc("TRN2", target_bir_lowering=False, num_devices=1)
    arrays, args = {}, []
    for name in _INS:
        a = np.ascontiguousarray(inputs[name])
        arrays[f"in_{name}"] = a
        args.append(nc.dram_tensor(f"in_{name}", a.shape, mybir.dt.from_np(a.dtype), kind="ExternalInput").ap())
    xp, xs, st, ck = (inputs[n].shape for n in ("x_prompt", "x_sample", "state_gla", "cache_k"))
    depth, heads = ck[0], ck[3:]
    outs = [xp, xs, (depth, xp[0]) + st[2:], st, (depth,) + xp[:2] + heads, (depth,) + xp[:2] + heads,
            (depth,) + xp[:2] + heads[:1], (depth,) + xs[:2] + heads, (depth,) + xs[:2] + heads,
            (depth,) + xs[:2] + heads[:1]]
    for n, shape in enumerate(outs):
        args.append(nc.dram_tensor(f"out_{n}", shape, F32, kind="ExternalOutput").ap())
    hybrid_step(nc, *args)
    r = run_bass_kernel_spmd(nc, [arrays], core_ids=[0])
    return tuple(r.results[0][f"out_{n}"] for n in range(len(outs)))
```
